# Optimizing a Trainium2 kernel written in Bass

```python
import math
import jax, jax.numpy as jnp
from jax import lax
import numpy as np

D_MODEL = 1024
BATCH = 1
SEQ = 512
DEPTH = 2
DEC_BATCH = 8
DEC_SEQ = 4
PAST_LEN = 4096
PAGE_SIZE = 128

N_MIXERS = 2
N_CONV_LAYERS = (DEPTH + 1) // 2
N_GLA_LAYERS = DEPTH // 2
D_FF = ((8 * D_MODEL // 3 + 255) // 256) * 256
CONV_WIDTH = 31
GLA_HEADS = 4
GLA_DK = D_MODEL // 2 // GLA_HEADS
GLA_DV = D_MODEL // GLA_HEADS
GLA_DKT = GLA_HEADS * GLA_DK
GLA_DVT = GLA_HEADS * GLA_DV
GLA_GATE_RANK = 16
GLA_TAU = 16.0
GLA_CHUNK = 32
EPS = 1e-6

kernel_name = 'macaron_conformer_conv_gla_hybrid_step'

def rms_norm(x, g):
    xf = x.astype(jnp.float32)
    y = xf * lax.rsqrt(jnp.mean(xf * xf, axis=-1, keepdims=True) + EPS)
    return (y * g.astype(jnp.float32)).astype(x.dtype)

def layer_norm(x, g, b):
    xf = x.astype(jnp.float32)
    mu = jnp.mean(xf, axis=-1, keepdims=True)
    var = jnp.mean(jnp.square(xf - mu), axis=-1, keepdims=True)
    y = (xf - mu) * lax.rsqrt(var + EPS) * g.astype(jnp.float32) + b.astype(jnp.float32)
    return y.astype(x.dtype)

def swiglu_ffn(h, w_gate, w_up, w_down):
    return (jax.nn.silu(h @ w_gate) * (h @ w_up)) @ w_down

def conv_module(h, state, w_pw1, b_pw1, w_dw, b_dw, ln_g, ln_b, w_pw2, b_pw2):
    u = h @ w_pw1 + b_pw1
    a, gate = jnp.split(u, 2, axis=-1)
    u = a * jax.nn.sigmoid(gate)
    full = jnp.concatenate([state.astype(u.dtype), u], axis=1)
    c = lax.conv_general_dilated(full, w_dw[:, None, :].astype(u.dtype), window_strides=(1,),
                                 padding='VALID', dimension_numbers=('NWC', 'WIO', 'NWC'),
                                 feature_group_count=D_MODEL) + b_dw
    c = jax.nn.silu(layer_norm(c, ln_g, ln_b))
    y = c @ w_pw2 + b_pw2
    new_state = full[:, -(CONV_WIDTH - 1):]
    return y, new_state

def gla_chunked(q, k, v, log_a, s0):
    B, L, H, DK = q.shape
    C = math.gcd(L, GLA_CHUNK)
    N = L // C
    r = lambda t: t.reshape(B, N, C, H, t.shape[-1])
    q, k, v, log_a = r(q), r(k), r(v), r(log_a)
    b = jnp.cumsum(log_a, axis=2)
    b_last = b[:, :, -1:]
    q_dec = q * jnp.exp(b)
    k_inv = k * jnp.exp(-b)
    k_end = k * jnp.exp(b_last - b)
    scores = jnp.einsum('bnchk,bnshk->bnhcs', q_dec, k_inv)
    mask = jnp.tril(jnp.ones((C, C), dtype=bool))
    scores = jnp.where(mask, scores, 0.0)
    o_intra = jnp.einsum('bnhcs,bnshv->bnchv', scores, v)

    def step(S, xs):
        qd, ke, vc, dl = xs
        o = jnp.einsum('bchk,bhkv->bchv', qd, S)
        S = S * jnp.exp(dl)[..., None] + jnp.einsum('bchk,bchv->bhkv', ke, vc)
        return S, o

    xs = (q_dec.swapaxes(0, 1), k_end.swapaxes(0, 1), v.swapaxes(0, 1), b_last[:, :, 0].swapaxes(0, 1))
    S, o_inter = lax.scan(step, s0, xs)
    o = o_intra + o_inter.swapaxes(0, 1)
    return o.reshape(B, L, H, v.shape[-1]), S

def gla_mixer(h, state, w_in, w_gate2, b_gate, g_onorm, w_out):
    B, L, _ = h.shape
    p = h @ w_in
    q, k, v, r, z = jnp.split(p, [GLA_DKT, 2 * GLA_DKT, 2 * GLA_DKT + GLA_DVT, 2 * GLA_DKT + 2 * GLA_DVT], axis=-1)
    log_a = jax.nn.log_sigmoid((z @ w_gate2 + b_gate).astype(jnp.float32)) / GLA_TAU
    hd = lambda t, d: t.astype(jnp.float32).reshape(B, L, GLA_HEADS, d)
    o, S = gla_chunked(hd(q, GLA_DK) * (GLA_DK ** -0.5), hd(k, GLA_DK), hd(v, GLA_DV),
                       log_a.reshape(B, L, GLA_HEADS, GLA_DK), state.astype(jnp.float32))
    o = o * lax.rsqrt(jnp.mean(o * o, axis=-1, keepdims=True) + EPS) * g_onorm.astype(jnp.float32)
    o = o.reshape(B, L, GLA_DVT).astype(h.dtype) * jax.nn.silu(r)
    return o @ w_out, S.astype(state.dtype)

def trunk(x, conv_state, gla_state, w):
    (norm_ffn_pre, norm_mix, norm_ffn_post, norm_final, ffn_w_gate, ffn_w_up, ffn_w_down,
     conv_w_pw1, conv_b_pw1, conv_w_dw, conv_b_dw, conv_ln_g, conv_ln_b, conv_w_pw2, conv_b_pw2,
     gla_w_in, gla_w_gate2, gla_b_gate, gla_onorm_g, gla_w_out) = w
    new_conv, new_gla = [], []
    for i in range(DEPTH):
        x = x + 0.5 * swiglu_ffn(rms_norm(x, norm_ffn_pre[i]), ffn_w_gate[i, 0], ffn_w_up[i, 0], ffn_w_down[i, 0])
        h = rms_norm(x, norm_mix[i])
        j = i // N_MIXERS
        if i % N_MIXERS == 0:
            y, s = conv_module(h, conv_state[j], conv_w_pw1[j], conv_b_pw1[j], conv_w_dw[j], conv_b_dw[j],
                               conv_ln_g[j], conv_ln_b[j], conv_w_pw2[j], conv_b_pw2[j])
            new_conv.append(s)
        else:
            y, s = gla_mixer(h, gla_state[j], gla_w_in[j], gla_w_gate2[j], gla_b_gate[j], gla_onorm_g[j], gla_w_out[j])
            new_gla.append(s)
        x = x + y
        x = x + 0.5 * swiglu_ffn(rms_norm(x, norm_ffn_post[i]), ffn_w_gate[i, 1], ffn_w_up[i, 1], ffn_w_down[i, 1])
    return rms_norm(x, norm_final), jnp.stack(new_conv), jnp.stack(new_gla)

def setup_inputs(seed: int = 0) -> dict:
    key = jax.random.key(seed)
    ks = iter(jax.random.split(key, 32))
    nrm = lambda shape, scale: jax.random.normal(next(ks), shape, jnp.float32) * scale
    gain = lambda shape: 1.0 + 0.02 * jax.random.normal(next(ks), shape, jnp.float32)
    d_in = 2 * GLA_DKT + 2 * GLA_DVT + GLA_GATE_RANK
    return {
        'x_prompt': nrm((BATCH, SEQ, D_MODEL), 1.0),
        'x_sample': nrm((DEC_BATCH, DEC_SEQ, D_MODEL), 1.0),
        'state_conv': nrm((N_CONV_LAYERS, DEC_BATCH, CONV_WIDTH - 1, D_MODEL), 0.5),
        'state_gla': nrm((N_GLA_LAYERS, DEC_BATCH, GLA_HEADS, GLA_DK, GLA_DV), 1.0),
        'norm_ffn_pre': gain((DEPTH, D_MODEL)),
        'norm_mix': gain((DEPTH, D_MODEL)),
        'norm_ffn_post': gain((DEPTH, D_MODEL)),
        'norm_final': gain((D_MODEL,)),
        'ffn_w_gate': nrm((DEPTH, 2, D_MODEL, D_FF), D_MODEL ** -0.5),
        'ffn_w_up': nrm((DEPTH, 2, D_MODEL, D_FF), D_MODEL ** -0.5),
        'ffn_w_down': nrm((DEPTH, 2, D_FF, D_MODEL), D_FF ** -0.5),
        'conv_w_pw1': nrm((N_CONV_LAYERS, D_MODEL, 2 * D_MODEL), D_MODEL ** -0.5),
        'conv_b_pw1': nrm((N_CONV_LAYERS, 2 * D_MODEL), 0.02),
        'conv_w_dw': nrm((N_CONV_LAYERS, CONV_WIDTH, D_MODEL), CONV_WIDTH ** -0.5),
        'conv_b_dw': nrm((N_CONV_LAYERS, D_MODEL), 0.02),
        'conv_ln_g': gain((N_CONV_LAYERS, D_MODEL)),
        'conv_ln_b': nrm((N_CONV_LAYERS, D_MODEL), 0.02),
        'conv_w_pw2': nrm((N_CONV_LAYERS, D_MODEL, D_MODEL), D_MODEL ** -0.5),
        'conv_b_pw2': nrm((N_CONV_LAYERS, D_MODEL), 0.02),
        'gla_w_in': nrm((N_GLA_LAYERS, D_MODEL, d_in), D_MODEL ** -0.5),
        'gla_w_gate2': nrm((N_GLA_LAYERS, GLA_GATE_RANK, GLA_DKT), GLA_GATE_RANK ** -0.5),
        'gla_b_gate': nrm((N_GLA_LAYERS, GLA_DKT), 0.1),
        'gla_onorm_g': gain((N_GLA_LAYERS, GLA_DV)),
        'gla_w_out': nrm((N_GLA_LAYERS, GLA_DVT, D_MODEL), GLA_DVT ** -0.5),
    }

def reference(x_prompt, x_sample, state_conv, state_gla,
              norm_ffn_pre, norm_mix, norm_ffn_post, norm_final, ffn_w_gate, ffn_w_up, ffn_w_down,
              conv_w_pw1, conv_b_pw1, conv_w_dw, conv_b_dw, conv_ln_g, conv_ln_b, conv_w_pw2, conv_b_pw2,
              gla_w_in, gla_w_gate2, gla_b_gate, gla_onorm_g, gla_w_out):
    w = (norm_ffn_pre, norm_mix, norm_ffn_post, norm_final, ffn_w_gate, ffn_w_up, ffn_w_down,
         conv_w_pw1, conv_b_pw1, conv_w_dw, conv_b_dw, conv_ln_g, conv_ln_b, conv_w_pw2, conv_b_pw2,
         gla_w_in, gla_w_gate2, gla_b_gate, gla_onorm_g, gla_w_out)
    b = x_prompt.shape[0]
    conv0 = jnp.zeros((N_CONV_LAYERS, b, CONV_WIDTH - 1, D_MODEL), x_prompt.dtype)
    gla0 = jnp.zeros((N_GLA_LAYERS, b, GLA_HEADS, GLA_DK, GLA_DV), x_prompt.dtype)
    y_prompt, new_conv_prompt, new_gla_prompt = trunk(x_prompt, conv0, gla0, w)
    y_sample, new_conv_sample, new_gla_sample = trunk(x_sample, state_conv, state_gla, w)
    return (y_prompt, y_sample, new_conv_prompt, new_gla_prompt, new_conv_sample, new_gla_sample)


_drawn_inputs = setup_inputs


def setup_inputs(seed=0):
    import zlib

    import numpy as np

    out = dict(_drawn_inputs(seed))
    spreads = {}
    factors = {'norm_ffn_pre': 3.729,
     'norm_ffn_post': 5.102,
     'norm_final': 8.195,
     'conv_ln_g': 10.227,
     'conv_ln_b': 10.649,
     'gla_onorm_g': 55.718,
     'conv_b_pw1': 2.698,
     'conv_b_pw2': 7.193}
    for name, (base, spread) in spreads.items():
        noise = np.random.default_rng([zlib.crc32(name.encode()), seed]).standard_normal(out[name].shape)
        drawn = base * np.exp(spread * noise) if base else spread * noise
        out[name] = __import__('jax').numpy.asarray(drawn.astype(out[name].dtype))
    for name, factor in factors.items():
        out[name] = (out[name] * factor).astype(out[name].dtype)
    return out
```

```python
from contextlib import ExitStack

import concourse.bass as bass
from concourse import mybir

ALU = mybir.AluOpType
ACT = mybir.ActivationFunctionType
AX_X = mybir.AxisListType.X
F32 = mybir.dt.float32
F32R = mybir.dt.float32r
I32 = mybir.dt.int32

P = 128
RING = 4
RAW = 2
AHEAD = 4
SLOT_K = 8


def build(nc, x_prompt, x_sample, state_conv, state_gla, norm_ffn_pre, norm_mix, norm_ffn_post, norm_final,
          ffn_w_gate, ffn_w_up, ffn_w_down, conv_w_pw1, conv_b_pw1, conv_w_dw, conv_b_dw, conv_ln_g, conv_ln_b,
          conv_w_pw2, conv_b_pw2, gla_w_in, gla_w_gate2, gla_b_gate, gla_onorm_g, gla_w_out,
          y_prompt, y_sample, new_conv_prompt, new_gla_prompt, new_conv_sample, new_gla_sample):
    _, SEQ, D = x_prompt.shape
    NB, DEC, _ = x_sample.shape
    NS = NB * DEC
    T = SEQ + NS
    HALF = T // 2
    M = D // P
    DFF = ffn_w_gate.shape[3]
    F = DFF // P
    TAPS = conv_w_dw.shape[1]
    HIST = TAPS - 1
    _, _, H, DK, DV = state_gla.shape
    RANK = gla_w_gate2.shape[1]
    CH = 32
    TAU = 16.0
    EPS = 1e-6
    TT = SEQ // P
    VB = DV // P
    HK, HV = H * DK, H * DV
    SEG = HIST + DEC
    UEXT = HIST + SEQ + NB * SEG
    assert D == 1024 and T == 544 and F == 22 and H == 4 and DK == P and DV == 2 * P and NS == 32

    ctx = ExitStack()
    with ctx:
        BASE = 16512
        taken = [BASE]

        def at(name, shape, dt, offset):
            return nc.alloc_sbuf_tensor_at(name, shape, dt, offset=offset)

        def sb(name, shape, dt=F32):
            n = 4
            for d in shape[1:]:
                n *= d
            offset = taken[0]
            taken[0] += (n + 31) // 32 * 32
            return at(name, shape, dt, offset)

        x = sb("x", [P, M, T])
        XG = taken[0]
        xg_hi = sb("xg_hi", [P, M, T], F32R)
        xg_lo = sb("xg_lo", [P, M, T], F32R)
        HHI = taken[0]
        h_hi = sb("h_hi", [P, F, T], F32R)
        HLO = taken[0]
        h_lo = sb("h_lo", [P, F, T], F32R)
        raw = sb("raw", [P, RAW, SLOT_K, P])
        w_hi = sb("w_hi", [P, RING, SLOT_K, P], F32R)
        w_lo = sb("w_lo", [P, RING, SLOT_K, P], F32R)
        ta = sb("ta", [P, 2, T])
        tb = sb("tb", [P, 2, T])
        rB = sb("rB", [P, T])
        nv = sb("nv", [P, T])
        ns = sb("ns", [P, T])
        acc = sb("acc", [P, T])
        SQT = taken[0]
        sqt = sb("sqt", [P, T])
        ident = sb("ident", [P, P])
        ones = sb("ones", [P, P])
        C_BPW1 = 7 * M
        C_BDW = C_BPW1 + 2 * M
        C_LNG = C_BDW + M
        C_LNB = C_LNG + M
        C_BPW2 = C_LNB + M
        C_BG = C_BPW2 + M
        C_ON = C_BG + H
        NPAR = C_ON + VB
        par = sb("par", [P, NPAR])
        wdw = sb("wdw", [P, TAPS * M])
        assert taken[0] <= 229344, taken[0]

        BLK = T * 4
        A0, B0 = HHI + M * BLK, HLO + M * BLK
        xin = at("xin", [P, TT + 1, D], F32, HHI)
        pin = at("pin", [P, P], F32, HLO)
        win = at("win", [P, 2, P], F32, HLO + 512)
        yout = at("yout", [P, TT + 1, D], F32, HHI)
        uext = at("uext", [P, M, UEXT], F32, A0)
        tail = at("tail", [P, M, HIST + NS], F32, A0 + M * UEXT * 4)
        cv = at("cv", [P, M, T], F32, B0)
        hist_in = at("hist_in", [P, 2, D], F32, B0 + M * BLK)
        prod = at("prod", [P, NS, TAPS], F32, B0 + M * BLK + 8192)
        tail_out = at("tail_out", [P, D], F32, B0 + M * BLK + 8192)
        PE_TAPS, POOL_TAPS = 6, 12
        DVE_TAP0 = 1 + PE_TAPS + POOL_TAPS
        STEPS = TAPS - DVE_TAP0 + 2
        PSUM_STEP = 6
        PRODS = 6
        diag = at("diag", [P, 2, PE_TAPS, P], F32, HHI)
        tap_prod = at("tap_prod", [P, PRODS, SEQ], F32, HLO)
        pool_sum = at("pool_sum", [P, 2, SEQ], F32, HLO + PRODS * SEQ * 4)
        rs = at("rs", [P, M, T], F32, HHI)
        G = P // CH
        v_tok = at("v_tok", [P, TT + 1, HV], F32, A0)
        o = A0 + (TT + 1) * HV * 4
        S = at("S", [P, 2, H, DV], F32, o)
        mask = at("mask", [P, 2, P], F32, o + 8192)
        bmask = at("bmask", [P, NB], F32, o + 9216)
        ssq = at("ssq", [P, TT + 1, H], F32, o + 9248)
        assert o + 9328 <= HLO
        la = at("la", [P, H, T], F32, HLO)
        bc = at("bc", [P, H, T], F32, HLO + H * BLK)
        q128 = at("q128", [P, 2, SEQ], F32, HLO)
        q64 = at("q64", [P, 2, TT, P // 2], F32, HLO + 4096)
        k64 = at("k64", [P, 2, TT, P // 2], F32, HLO + 6144)
        kem = at("kem", [P, NB, H, DK], F32, HLO + 1024)
        q32 = at("q32", [P, 2, T], F32, B0)
        zr = at("zr", [P, T], F32, B0)
        kinv = at("kinv", [P, 2, T], F32, B0 + 2 * BLK)
        k32 = at("k32", [P, 2, T], F32, B0 + 4 * BLK)
        o = B0 + 6 * BLK
        kend_tok = at("kend_tok", [P, 2, TT, DK], F32, o)
        kend_s = at("kend_s", [P, H, DK], F32, o + 4096)
        SEL = NS + DEC
        qsel = at("qsel", [P, H, NB * SEL], F32, o + 6144)
        msc = at("msc", [P, 2, P], F32, o + 10752)
        smsc = at("smsc", [P, H, NS], F32, o + 11776)
        smask = at("smask", [P, NS], F32, o + 12288)
        reset = at("reset", [P, T], F32, o + 12416)
        wg2 = at("wg2", [P, HK], F32, o + 14592)
        dec = at("dec", [P, H, NB], F32, o + 16640)
        assert o + 16768 <= B0 + (F - M) * BLK
        F_E, F_R, F_X = 0, G + 1, 2 * G + 1
        fac = at("fac", [P, H, TT, 3 * G + 1], F32, SQT)
        st = at("st", [P, H, NB, DV], F32, XG)

        ps = nc.alloc_psum_tensor("ps", [P, 8, 512], F32)

        def bank_pair(pair):
            return ps[:, 2 * pair:2 * pair + 2, 0:HALF]

        def halves(ap):
            return ap.rearrange("p (c n) -> p c n", c=2)

        def sem(name):
            return ctx.enter_context(nc.semaphore(name))

        s_const = sem("s_const")
        s_in = sem("s_in")
        s_par = sem("s_par")
        s_parc = sem("s_parc")
        w_loaded = [sem(f"w_loaded{r}") for r in range(RAW)]
        w_high = sem("w_high")
        w_split = sem("w_split")
        w_done = sem("w_done")
        u_init = sem("u_init")
        evac = sem("evac")
        a_done = sem("a_done")
        h_prod = sem("h_prod")
        h_high = sem("h_high")
        h_split = sem("h_split")
        x_high = sem("x_high")
        x_split = sem("x_split")
        p_acc = sem("p_acc")
        s_acc = sem("s_acc")
        s_stat = sem("s_stat")
        s_nv = sem("s_nv")
        s_sqrt = sem("s_sqrt")
        s_rb = sem("s_rb")
        c_hist = sem("c_hist")
        c_zero = sem("c_zero")
        c_tr = sem("c_tr")
        c_tre = sem("c_tre")
        c_u = sem("c_u")
        c_tap0 = sem("c_tap0")
        c_diag = sem("c_diag")
        c_prod = sem("c_prod")
        c_padd = sem("c_padd")
        c_pe = sem("c_pe")
        c_tap = sem("c_tap")
        c_samp = sem("c_samp")
        c_mu = sem("c_mu")
        c_mean = sem("c_mean")
        c_sq = sem("c_sq")
        c_var = sem("c_var")
        c_norm = sem("c_norm")
        c_tail = sem("c_tail")
        c_tt = sem("c_tt")
        c_tte = sem("c_tte")
        c_out = sem("c_out")
        g_const = sem("g_const")
        g_in = sem("g_in")
        g_tr = sem("g_tr")
        g_tre = sem("g_tre")
        g_mm = sem("g_mm")
        g_abs = sem("g_abs")
        g_min = sem("g_min")
        g_fac = sem("g_fac")
        g_exp = sem("g_exp")
        g_dec = sem("g_dec")
        g_kq = sem("g_kq")
        g_sc = sem("g_sc")
        g_kv = sem("g_kv")
        g_msk = sem("g_msk")
        g_S = sem("g_S")
        g_o = sem("g_o")
        g_oe = sem("g_oe")
        g_st = [sem(f"g_st{h}") for h in range(H)]
        g_kem = sem("g_kem")
        g_ssc = sem("g_ssc")
        g_smk = sem("g_smk")
        g_so = sem("g_so")
        g_soe = sem("g_soe")
        g_skv = sem("g_skv")
        g_sS = sem("g_sS")
        g_on = sem("g_on")
        g_ot = sem("g_ot")
        g_y = sem("g_y")
        g_out = sem("g_out")
        f_y = sem("f_y")
        f_tr = sem("f_tr")
        f_e = sem("f_e")
        f_out = sem("f_out")

        class Stage:
            pass

        count = {"slot": 0, "unit": M, "h": 0, "act": 0, "prod": 0}

        def stage(slots, units):
            s = Stage()
            s.s0, s.u0 = count["slot"], count["unit"]
            count["slot"] += slots
            count["unit"] += units
            return s

        def ffn(layer, which, q, e, r):
            s = Stage()
            s.up, s.down = stage(2 * F, 2 * F), stage(3 * M, M)
            s.layer, s.which, s.q, s.e, s.r = layer, which, q, e, r
            s.h0, s.a0, s.p0 = count["h"], count["act"], count["prod"]
            count["h"] += F
            count["act"] += F
            count["prod"] += F
            return s

        f00 = ffn(0, 0, 0, 0, 0)
        pw1 = stage(2 * M, 2 * M)
        conv_h0, conv_a0 = count["h"], count["act"]
        count["h"] += M
        count["act"] += 2 * M
        pw2 = stage(M, M)
        f01 = ffn(0, 1, 2, 2, 3)
        f10 = ffn(1, 0, 3, 3, 4)
        gz = stage(1, 1)
        gv, gr, gkq = stage(M, M), stage(M, M), stage(2 * H, 2 * H)
        gla_a0, gla_h0 = count["act"], count["h"]
        count["act"] += M
        count["h"] += M
        gwo = stage(M, M)
        f11 = ffn(1, 1, 5, 5, 7)
        SLOTS = count["slot"]
        GN = gz.u0
        AUX0, AUX1 = (GN + 2) % 4, (GN + 3) % 4

        def gpair(u):
            return (GN + (u - GN) % 2) % 4

        KQ = 10
        KQP = AUX1
        T_BANK, KV_BANK = 2 * AUX0, 2 * AUX0 + 1

        def sc_bank(y):
            return 2 * (GN % 4) + y

        def o_bank(y):
            return 2 * ((GN + 1) % 4) + y

        def skv_bank(s):
            return (sc_bank(0), sc_bank(1), 2 * KQP, 2 * KQP + 1)[s % 4]

        def wait(eng, semaphore, value):
            if not isinstance(value, int) or value > 0:
                eng.wait_ge(semaphore, value)

        def load_slot(sp, j, i, per, source):
            wait(sp, w_split, j + per * i - RAW + 1)
            nk = source.shape[0] // P
            sp.dma_start(raw[:, j % RAW, 0:nk, :], source.rearrange("(k p) m -> p k m", p=P)).then_inc(
                w_loaded[j % RAW], 16)

        def load_ffn(sp, s):
            gate, up, down = (w[s.layer, s.which] for w in (ffn_w_gate, ffn_w_up, ffn_w_down))
            if s is f00:
                for m in range(2):
                    for g, w in enumerate((gate, up)):
                        load_slot(sp, s.up.s0 + 2 * m + g, 0, 0, w[:, m * P:(m + 1) * P])
            with sp.Fori(1 if s is f00 else 0, F // 2) as i:
                for p in range(2):
                    for g, w in enumerate((gate, up)):
                        load_slot(sp, s.up.s0 + 2 * p + g, i, 4, w[:, bass.ts(2 * i + p, P)])
            with sp.Fori(0, M // 2) as i:
                for p in range(2):
                    for j in range(3):
                        rows = down[j * SLOT_K * P:min((j + 1) * SLOT_K, F) * P, :]
                        load_slot(sp, s.down.s0 + 3 * p + j, i, 6, rows[:, bass.ts(2 * i + p, P)])

        def load_square(sp, s, w, col0=0, blocks=M):
            with sp.Fori(0, blocks // 2) as i:
                for p in range(2):
                    load_slot(sp, s.s0 + p, i, 2, w[:, bass.ds(col0 + (2 * i + p) * P, P)])

        def high(act, n, i=0, per=0):
            if n >= SLOTS:
                return
            act.wait_ge(w_loaded[n % RAW], 16 * (n // RAW + 1) + 16 * (per // RAW) * i)
            wait(act, w_done, n - RING + 1 + per * i)
            nc.scalar.activation(w_hi[:, n % RING], raw[:, n % RAW], ACT.Copy).then_inc(w_high, 1)

        def low(dve, n, i=0, per=0):
            if n >= SLOTS:
                return
            dve.wait_ge(w_high, n + 1 + per * i)
            nc.vector.tensor_tensor(w_lo[:, n % RING], raw[:, n % RAW], w_hi[:, n % RING].bitcast(F32),
                                    ALU.subtract).then_inc(w_split, 1)

        def slot_products(pe, n, pair, a_hi, a_lo, nk=SLOT_K, k0=0, kt=SLOT_K, i=0, per=0, ready=None):
            pe.wait_ge(w_split, n + 1 + per * i)
            r = n % RING
            for k in range(nk):
                if ready is not None:
                    pe.wait_ge(ready[0], ready[1] + k + 1)
                for w, a in ((w_hi, a_hi), (w_hi, a_lo), (w_lo, a_hi)):
                    for c in range(2):
                        last = nc.tensor.matmul(
                            ps[:, 2 * pair + c, 0:HALF], w[:, r, k, :], a[:, k0 + k, c * HALF:(c + 1) * HALF],
                            start=(k0 + k == 0 and w is w_hi and a is a_hi),
                            stop=(k0 + k == kt - 1 and w is w_lo))
            last.then_inc(w_done, 1)

        def pe_stat(pe, e, pair, free=None):
            pe.wait_ge(s_acc, e + 1)
            for c in range(2):
                last = nc.tensor.matmul(ps[:, 2 * pair + c, 0:HALF], ones[:, :], acc[:, c * HALF:(c + 1) * HALF],
                                        start=True, stop=True)
            last.then_inc(s_stat, 1)

        def pe_ffn(pe, s):
            u0, s0 = s.up.u0, s.up.s0
            for j in range(4):
                wait(pe, evac, u0 + j - 3)
                if j == 3:
                    pe.wait_ge(s_nv, 4 * s.r + 1)
                slot_products(pe, s0 + j, (u0 + j) % 4, xg_hi, xg_lo, ready=(x_split, M * s.q) if j == 0 else None)
                if j == 0:
                    pe_stat(pe, s.e, (u0 + 3) % 4)
            with pe.Fori(1, F // 2) as i:
                for j in range(4):
                    pe.wait_ge(evac, u0 + j - 3 + 4 * i)
                    slot_products(pe, s0 + j, (u0 + j) % 4, xg_hi, xg_lo, i=i, per=4)
            u0, s0 = s.down.u0, s.down.s0
            with pe.Fori(0, M // 4) as i:
                for j in range(4):
                    pe.wait_ge(evac, u0 + j - 3 + 4 * i)
                    for c in range(3):
                        k0 = c * SLOT_K
                        slot_products(pe, s0 + 3 * j + c, (u0 + j) % 4, h_hi, h_lo, nk=min(SLOT_K, F - k0), k0=k0,
                                      kt=F, i=i, per=12, ready=(h_split, s.h0 + k0) if j == 0 else None)

        def pe_square(pe, s, a_hi, a_lo, ready):
            with pe.Fori(0, M // 4) as i:
                for j in range(4):
                    pe.wait_ge(evac, s.u0 + j - 3 + 4 * i)
                    slot_products(pe, s.s0 + j, (s.u0 + j) % 4, a_hi, a_lo, i=i, per=4,
                                  ready=ready if j == 0 else None)

        def act_x_high(act, unit, q, m):
            act.wait_ge(evac, unit + 1)
            if q < 6:
                nc.scalar.activation(xg_hi[:, m, :], x[:, m, :], ACT.Copy,
                                     scale=par[:, bass.ds(q * M + m, 1)]).then_inc(x_high, 1)

        def dve_x_split(dve, q, m):
            if q < 6:
                dve.wait_ge(x_high, M * q + m + 1)
                nc.vector.scalar_tensor_tensor(
                    out=xg_lo[:, m, :], in0=x[:, m, :], scalar=par[:, bass.ds(q * M + m, 1)],
                    in1=xg_hi[:, m, :].bitcast(F32), op0=ALU.mult, op1=ALU.subtract).then_inc(x_split, 1)

        pool_steps = [0]

        def pool_square_sum(pool, src, e, ready):
            for m in range(M):
                pool.wait_ge(*ready(m))
                if m == 0:
                    wait(pool, s_stat, e)
                    nc.gpsimd.tensor_tensor(acc[:, :], src[:, m, :], src[:, m, :], ALU.mult).then_inc(p_acc, 1)
                    pool_steps[0] += 1
                    continue
                pool.wait_ge(p_acc, pool_steps[0])
                nc.gpsimd.tensor_tensor(sqt[:, :], src[:, m, :], src[:, m, :], ALU.mult).then_inc(p_acc, 1)
                pool_steps[0] += 1
                pool.wait_ge(p_acc, pool_steps[0])
                last = nc.gpsimd.tensor_tensor(acc[:, :], acc[:, :], sqt[:, :], ALU.add)
                if m < M - 1:
                    last.then_inc(p_acc, 1)
                    pool_steps[0] += 1
                else:
                    last.then_inc(s_acc, 1)

        def dve_rsqrt(dve, r, pair, stat, n=T):
            dve.wait_ge(*stat)
            if pair is None:
                nc.vector.tensor_scalar(nv[:, 0:n], ssq[:, :, :].rearrange("p t h -> p (t h)"), 1.0 / DV, EPS, ALU.mult,
                                        ALU.add).then_inc(s_nv, 1)
            else:
                nc.vector.tensor_scalar(halves(nv[:, :]), bank_pair(pair), EPS, None, ALU.add).then_inc(s_nv, 1)
            dve.wait_ge(s_sqrt, r + 1)
            nc.vector.reciprocal(rB[:, 0:n], ns[:, 0:n]).then_inc(s_nv, 1)
            dve.wait_ge(s_nv, 4 * r + 2)
            nc.vector.scalar_tensor_tensor(out=ns[:, 0:n], in0=rB[:, 0:n], scalar=-0.5, in1=rB[:, 0:n], op0=ALU.mult,
                                           op1=ALU.mult).then_inc(s_nv, 1)
            dve.wait_ge(s_nv, 4 * r + 3)
            nc.vector.tensor_tensor(ns[:, 0:n], ns[:, 0:n], nv[:, 0:n], ALU.mult).then_inc(s_nv, 1)
            dve.wait_ge(s_nv, 4 * r + 4)
            nc.vector.scalar_tensor_tensor(out=rB[:, 0:n], in0=ns[:, 0:n], scalar=1.5, in1=rB[:, 0:n], op0=ALU.add,
                                           op1=ALU.mult).then_inc(s_rb, 1)
            dve.wait_ge(s_rb, r + 1)

        def act_sqrt(act, r, n=T):
            act.wait_ge(s_nv, 4 * r + 1)
            nc.scalar.activation(ns[:, 0:n], nv[:, 0:n], ACT.Sqrt).then_inc(s_sqrt, 1)

        def act_ffn(act, s):
            act_sqrt(act, s.r)
            s0, u0 = s.up.s0, s.up.u0
            act.preload_act_table(ACT.Silu)
            with act.Fori(0, F // 2) as i:
                for p in range(2):
                    high(act, s0 + 2 * p + AHEAD, i, 4)
                    act.wait_ge(evac, u0 + 2 * p + 1 + 4 * i)
                    nc.scalar.activation(ta[:, p, :], ta[:, p, :], ACT.Silu).then_inc(a_done, 1)
                    high(act, s0 + 2 * p + 1 + AHEAD, i, 4)
                    act.wait_ge(h_prod, s.p0 + p + 1 + 2 * i)
                    nc.scalar.activation(h_hi[:, 2 * i + p, :], tb[:, p, :], ACT.Copy).then_inc(h_high, 1)
            s0, u0 = s.down.s0, s.down.u0

            def body(i):
                for j in range(4):
                    for c in range(3):
                        high(act, s0 + 3 * j + c + AHEAD, i, 12)
                    act_x_high(act, u0 + j + 4 * i, s.q + 1, j + 4 * i)

            if s is f11:
                for j in range(M):
                    for c in range(3):
                        high(act, s0 + 3 * j + c + AHEAD)
            else:
                with act.Fori(0, M // 4) as i:
                    body(i)

        def dve_ffn(dve, s):
            dve_rsqrt(dve, s.r, (s.up.u0 + 3) % 4, (s_stat, s.e + 1))
            s0, u0 = s.up.s0, s.up.u0
            with dve.Fori(0, F // 2) as i:
                for p in range(2):
                    n = s0 + 2 * p
                    pair = (u0 + 2 * p) % 4
                    dve.wait_ge(w_done, n + 1 + 4 * i)
                    nc.vector.tensor_tensor(halves(ta[:, p, :]), bank_pair(pair), halves(rB[:, :]),
                                            ALU.mult).then_inc(evac, 1)
                    low(dve, n + AHEAD, i, 4)
                    dve.wait_ge(w_done, n + 2 + 4 * i)
                    nc.vector.tensor_tensor(halves(tb[:, p, :]), bank_pair((pair + 1) % 4), halves(rB[:, :]),
                                            ALU.mult).then_inc(evac, 1)
                    low(dve, n + 1 + AHEAD, i, 4)
                    dve.wait_ge(a_done, s.a0 + p + 1 + 2 * i)
                    dve.wait_ge(evac, u0 + 2 * p + 2 + 4 * i)
                    nc.vector.tensor_tensor(tb[:, p, :], ta[:, p, :], tb[:, p, :], ALU.mult).then_inc(h_prod, 1)
                    dve.wait_ge(h_high, s.h0 + p + 1 + 2 * i)
                    nc.vector.tensor_tensor(h_lo[:, 2 * i + p, :], tb[:, p, :], h_hi[:, 2 * i + p, :].bitcast(F32),
                                            ALU.subtract).then_inc(h_split, 1)
            s0, u0 = s.down.s0, s.down.u0

            def body(i):
                for j in range(4):
                    m = j + 4 * i
                    for c in range(3):
                        low(dve, s0 + 3 * j + c + AHEAD, i if s is not f11 else 0, 12)
                    dve.wait_ge(w_done, s0 + 3 * j + 3 + 12 * i)
                    nc.vector.scalar_tensor_tensor(
                        out=halves(x[:, m, :]), in0=bank_pair((u0 + j) % 4), scalar=0.5,
                        in1=halves(x[:, m, :]), op0=ALU.mult, op1=ALU.add).then_inc(evac, 1)
                    dve_x_split(dve, s.q + 1, m)

            if s is f11:
                for m in range(M):
                    for c in range(3):
                        low(dve, s0 + 3 * m + c + AHEAD)
                    dve.wait_ge(w_done, s0 + 3 * m + 3)
                    nc.vector.scalar_tensor_tensor(
                        out=halves(x[:, m, :]), in0=bank_pair((u0 + m) % 4), scalar=0.5,
                        in1=halves(x[:, m, :]), op0=ALU.mult, op1=ALU.add).then_inc(evac, 1)
            else:
                with dve.Fori(0, M // 4) as i:
                    body(i)

        norms = [norm_ffn_pre[0], norm_mix[0], norm_ffn_post[0], norm_ffn_pre[1], norm_mix[1], norm_ffn_post[1],
                 norm_final]
        PAR_ROWS = [(q * M, v) for q, v in enumerate(norms)] + [
            (C_BPW1, conv_b_pw1[0]), (C_BDW, conv_b_dw[0]), (C_LNG, conv_ln_g[0]), (C_LNB, conv_ln_b[0]),
            (C_BPW2, conv_b_pw2[0]), (C_BG, gla_b_gate[0]), (C_ON, gla_onorm_g[0])]
        PAR_DMAS = len(PAR_ROWS) + 4

        def by_chunk(ap):
            return ap.rearrange("p (t g c) -> p t g c", g=G, c=CH)

        def factor(h, first, t0=0, n=G):
            f = fac[:, h, t0:TT, first:first + n].rearrange("p t (g o) -> p t g o", o=1)
            return f.to_broadcast([P, TT - t0, n, CH])

        def tap(j, m):
            return wdw[:, j * M + m:j * M + m + 1]

        def squares(b):
            return (ta if b % 4 < 2 else tb)[:, b % 2, :]

        block = ctx.enter_context(nc.Block())

        @block.sync
        def _(sp):
            load_ffn(sp, f00)
            with sp.Fori(0, M // 2) as i:
                for p in range(2):
                    for g in range(2):
                        load_slot(sp, pw1.s0 + 2 * p + g, i, 4, conv_w_pw1[0, :, bass.ds(g * D + (2 * i + p) * P, P)])
            load_square(sp, pw2, conv_w_pw2[0])
            load_ffn(sp, f01)
            load_ffn(sp, f10)
            load_slot(sp, gz.s0, 0, 0, gla_w_in[0, :, 2 * HK + 2 * HV + RANK - P:2 * HK + 2 * HV + RANK])
            load_square(sp, gv, gla_w_in[0], 2 * HK)
            load_square(sp, gr, gla_w_in[0], 2 * HK + HV)
            for h in range(H):
                for g in range(2):
                    load_slot(sp, gkq.s0 + 2 * h + g, 0, 0,
                              gla_w_in[0, :, (1 - g) * HK + h * DK:(1 - g) * HK + (h + 1) * DK])
            load_square(sp, gwo, gla_w_out[0])
            load_ffn(sp, f11)
            for t in range(TT + 1):
                sp.wait_ge(f_e, t + 1)
                if t < TT:
                    sp.dma_start(y_prompt[0, t * P:(t + 1) * P, :], yout[:, t, :]).then_inc(f_out, 16)
                else:
                    sp.dma_start(y_sample.rearrange("b t d -> (b t) d"), yout[0:NS, t, :]).then_inc(f_out, 16)
            sp.wait_ge(f_out, 16 * (TT + 1))
            sp.wait_ge(c_out, 16 * 4)
            sp.wait_ge(g_out, 16 * (H + 1))

        @block.gpsimd
        def _(pool):
            nc.gpsimd.memset(ident[:, :], 0.0).then_inc(s_const, 1)
            nc.gpsimd.memset(ones[:, :], 1.0 / D).then_inc(s_const, 1)
            pool.wait_ge(s_const, 2)
            nc.gpsimd.affine_select(out=ident[:, :], in_=ident[:, :], compare_op=ALU.not_equal, fill=1.0, base=0,
                                    pattern=[[-1, P]], channel_multiplier=1).then_inc(s_const, 1)
            pool_square_sum(pool, x, 0, lambda m: (evac, m + 1))
            pool_square_sum(pool, x, 1, lambda m: (evac, f00.down.u0 + m + 1))
            pool.dma_start(new_conv_sample[0, :, 0:HIST - DEC, :], state_conv[0, :, DEC:HIST, :]).then_inc(c_out, 16)
            pool.wait_ge(w_done, pw1.s0)
            for b in range(2):
                pool.dma_start(hist_in[0:NB // 2 * HIST, b, :],
                               state_conv[0, b * NB // 2:(b + 1) * NB // 2, :, :].rearrange("b t d -> (b t) d")
                               ).then_inc(c_hist, 16)
            nc.gpsimd.memset(uext[:, :, 0:HIST], 0.0).then_inc(c_zero, 1)
            for m in range(M):
                for j in range(1, POOL_TAPS):
                    k = m * (POOL_TAPS - 1) + j - 1
                    pool.wait_ge(c_prod, m * POOL_TAPS + j + 1)
                    if j > 1:
                        pool.wait_ge(c_padd, k)
                    nc.gpsimd.tensor_tensor(pool_sum[:, m % 2, :], pool_sum[:, m % 2, :], tap_prod[:, k % PRODS, :],
                                            ALU.add).then_inc(c_padd, 1)
            pool.wait_ge(c_tte, 2)
            pool.dma_start(new_conv_prompt[0, 0, :, :], tail_out[0:HIST, :]).then_inc(c_out, 16)
            for b in range(2):
                n = NS // 2
                pool.dma_start(new_conv_sample[0, b * NB // 2:(b + 1) * NB // 2, HIST - DEC:HIST, :],
                               tail_out[HIST + b * n:HIST + (b + 1) * n, :]).then_inc(c_out, 16)
            pool.wait_ge(c_out, 64)
            pool_square_sum(pool, x, 2, lambda m: (evac, pw2.u0 + m + 1))
            pool_square_sum(pool, x, 3, lambda m: (evac, f01.down.u0 + m + 1))
            pool_square_sum(pool, x, 4, lambda m: (evac, f10.down.u0 + m + 1))
            pool.wait_ge(w_done, gz.s0)
            for buffer, value in ((wg2[:, :], 0.0), (reset[:, :], 1.0), (mask[:, 0, :], 1.0), (mask[:, 1, :], 0.0),
                                  (smask[:, :], 1.0), (bmask[:, :], 1.0), (v_tok[:, TT, :], 0.0), (kend_s[:, :, :], 0.0), (qsel[:, :, :], 0.0),
                                  (msc[:, :, :], 0.0), (smsc[:, :, :], 0.0), (ssq[:, :, :], 0.0)):
                nc.gpsimd.memset(buffer, value).then_inc(g_const, 1)
            pool.wait_ge(g_const, 12)
            pool.dma_start(wg2[P - RANK:P, :], gla_w_gate2[0]).then_inc(g_in, 16)
            nc.gpsimd.memset(reset[:, 0:SEQ:CH], 0.0).then_inc(g_const, 1)
            nc.gpsimd.memset(reset[:, SEQ:T:DEC], 0.0).then_inc(g_const, 1)
            pool.wait_ge(s_acc, 5)
            nc.gpsimd.memset(fac[:, :, :, :], 0.0).then_inc(g_const, 1)
            odd = mask[:, 1, :].rearrange("p (a u c) -> p a u c", a=2, u=2)[:, :, 1, :]
            nc.gpsimd.memset(odd, 1.0).then_inc(g_const, 1)
            pool.wait_ge(g_const, 16)
            nc.gpsimd.affine_select(out=odd, in_=odd, compare_op=ALU.is_ge, fill=0.0, base=0,
                                    pattern=[[-2 * CH, 2], [0, CH]], channel_multiplier=1).then_inc(g_const, 1)
            nc.gpsimd.affine_select(out=mask[:, 0, :], in_=mask[:, 0, :], compare_op=ALU.is_ge, fill=0.0, base=0,
                                    pattern=[[1, P]], channel_multiplier=-1).then_inc(g_const, 1)
            nc.gpsimd.affine_select(out=smask[:, :], in_=smask[:, :], compare_op=ALU.is_ge, fill=0.0, base=0,
                                    pattern=[[1, NS]], channel_multiplier=-1).then_inc(g_const, 1)
            nc.gpsimd.affine_select(out=bmask[:, :], in_=bmask[:, :], compare_op=ALU.is_ge, fill=0.0, base=0,
                                    pattern=[[-DEC, NB]], channel_multiplier=1).then_inc(g_const, 1)
            pool.wait_ge(g_const, 20)
            nc.gpsimd.affine_select(out=odd, in_=odd, compare_op=ALU.is_ge, fill=0.0, base=CH - 1,
                                    pattern=[[2 * CH, 2], [0, CH]], channel_multiplier=-1).then_inc(g_const, 1)
            mv = mask[:, 0, :].rearrange("p (b c) -> p b c", c=CH)
            nc.gpsimd.affine_select(out=mv, in_=mv, compare_op=ALU.is_ge, fill=0.0, base=0,
                                    pattern=[[-CH, P // CH], [0, CH]], channel_multiplier=1).then_inc(g_const, 1)
            mv = smask[:, :].rearrange("p (b c) -> p b c", c=DEC)
            nc.gpsimd.affine_select(out=mv, in_=mv, compare_op=ALU.is_ge, fill=0.0, base=0,
                                    pattern=[[-DEC, NB], [0, DEC]], channel_multiplier=1).then_inc(g_const, 1)
            nc.gpsimd.affine_select(out=bmask[:, :], in_=bmask[:, :], compare_op=ALU.is_ge, fill=0.0, base=DEC - 1,
                                    pattern=[[DEC, NB]], channel_multiplier=-1).then_inc(g_const, 1)
            pool.wait_ge(w_done, gkq.s0 + 2 * H)
            for h in range(H):
                pool.dma_start(st[:, h], state_gla[0, :, h].rearrange("b k v -> k b v")).then_inc(g_st[h], 16)
            pool.wait_ge(g_S, TT * H)
            pool.dma_start(new_gla_prompt[0, 0].rearrange("h k v -> k h v"), S[:, TT % 2]).then_inc(g_out, 16)
            for h in range(H):
                pool.wait_ge(g_sS, NB * (h + 1))
                pool.dma_start(new_gla_sample[0, :, h].rearrange("b k v -> k b v"), st[:, h]).then_inc(g_out, 16)
            pool_square_sum(pool, x, 5, lambda m: (evac, gwo.u0 + m + 1))
            pool_square_sum(pool, x, 6, lambda m: (evac, f11.down.u0 + m + 1))

        @block.tensor
        def _(pe):
            pe.wait_ge(s_const, 3)
            pe.wait_ge(s_in, 16 * PAR_DMAS)
            nc.tensor.transpose(ps[:, 6, 0:NPAR], pin[0:NPAR, :], ident[0:NPAR, 0:NPAR])
            for b in range(2):
                n = TAPS * M // 2
                last = nc.tensor.transpose(ps[:, 7, b * n:(b + 1) * n], win[0:n, b, :], ident[0:n, 0:n])
            last.then_inc(s_par, 1)
            for m in range(M):
                wait(pe, evac, m - 3)
                if m == 3:
                    pe.wait_ge(s_parc, 2)
                for t in range(TT):
                    nc.tensor.transpose(ps[:, 2 * (m % 4), t * P:(t + 1) * P], xin[:, t, m * P:(m + 1) * P],
                                        ident[:, :])
                nc.tensor.transpose(ps[:, 2 * (m % 4) + 1, 0:NS], xin[0:NS, TT, m * P:(m + 1) * P],
                                    ident[0:NS, 0:NS]).then_inc(u_init, 1)
            pe_ffn(pe, f00)

            def taps(m):
                pe.wait_ge(c_u, m + 1)
                pe.wait_ge(c_diag, m + 1)
                if m >= 2:
                    pe.wait_ge(c_tap, (m - 2) * 2 * STEPS + 2 * PSUM_STEP + 2)
                for j in range(1, PE_TAPS + 1):
                    last = nc.tensor.matmul(ps[:, 4 + m % 2, :], diag[:, m % 2, j - 1, :], uext[:, m, j:j + SEQ],
                                            start=(j == 1), stop=(j == PE_TAPS))
                last.then_inc(c_pe, 1)

            def moment(m, pair, src, done):
                for c in range(2):
                    last = nc.tensor.matmul(ps[:, 2 * pair + c, 0:HALF], ones[:, :], src[:, c * HALF:(c + 1) * HALF],
                                            start=(m == 0), stop=(m == M - 1))
                last.then_inc(done, 1)

            def mean(m):
                pe.wait_ge(c_tap, (m + 1) * 2 * STEPS)
                pe.wait_ge(c_samp, 3 * (m + 1))
                moment(m, 3, cv[:, m, :], c_mu)

            u0, s0 = pw1.u0, pw1.s0
            assert u0 % 4 == 0
            for j in range(2):
                pe.wait_ge(evac, u0 + j - 3)
                slot_products(pe, s0 + j, j, xg_hi, xg_lo, ready=(x_split, M) if j == 0 else None)
                if j == 0:
                    pe_stat(pe, 1, 3)
            n = NB // 2 * HIST
            pe.wait_ge(c_hist, 32)
            for m in range(M):
                wait(pe, c_tre, 2 * (m // 4))
                for b in range(2):
                    col = (m % 2) * 2 * n + b * n
                    last = nc.tensor.transpose(ps[:, 4 + m % 4 // 2, col:col + n],
                                               hist_in[0:n, b, m * P:(m + 1) * P], ident[0:n, 0:n])
                if m % 2:
                    last.then_inc(c_tr, 1)
            for m in range(1, M):
                for g in range(2):
                    j = 2 * m + g
                    pe.wait_ge(evac, u0 + j - 1)
                    slot_products(pe, s0 + j, g, xg_hi, xg_lo)
                if m == 1:
                    pe.wait_ge(c_tre, 4)
                taps(m - 1)
                if m == 2:
                    pe.wait_ge(s_nv, 4 * 1 + 1)
                if m >= 2:
                    mean(m - 2)
            taps(M - 1)
            pe.wait_ge(evac, pw2.u0)
            pe.wait_ge(c_tail, M)
            for m in range(M):
                last = nc.tensor.transpose(ps[0:HIST + NS, 2 + m // 4, (m % 4) * P:(m % 4 + 1) * P],
                                           tail[:, m, :], ident[:, :])
            last.then_inc(c_tt, 1)
            mean(M - 2)
            mean(M - 1)
            for m in range(M):
                pe.wait_ge(c_sq, m + 1)
                moment(m, 0, squares(m), c_var)
            pe.wait_ge(c_tte, 2)
            pe.wait_ge(s_nv, 4 * 2 + 1)
            pe_square(pe, pw2, h_hi, h_lo, (h_split, conv_h0))

            pe_ffn(pe, f01)
            pe_ffn(pe, f10)

            pe.wait_ge(evac, GN - 3)
            slot_products(pe, gz.s0, gpair(gz.u0), xg_hi, xg_lo, ready=(x_split, 4 * M))
            pe.wait_ge(evac, GN)
            pe_stat(pe, 4, AUX1)

            def transposes(k, src):
                wait(pe, g_tre, 2 * k)
                for t in range(TT):
                    nc.tensor.transpose(ps[:, 2 * AUX0, t * P:(t + 1) * P], src[:, t * P:(t + 1) * P], ident[:, :])
                nc.tensor.transpose(ps[0:NS, 2 * AUX0 + 1, 0:P], src[:, SEQ:T], ident[:, :]).then_inc(g_tr, 1)

            for j in range(M):
                pe.wait_ge(evac, gv.u0 + j - 1)
                slot_products(pe, gv.s0 + j, gpair(gv.u0 + j), xg_hi, xg_lo)
                if j:
                    pe.wait_ge(evac, gv.u0 + j)
                    transposes(j - 1, ta[:, (j - 1) % 2, :])
            pe.wait_ge(evac, gv.u0 + M)
            transposes(M - 1, ta[:, (M - 1) % 2, :])
            pe.wait_ge(g_in, 16)
            pe.wait_ge(s_nv, 4 * 5 + 1)
            pe.wait_ge(g_tre, 2 * M)
            for h in range(H):
                pair = (AUX1, AUX0)[h % 2]
                if h >= 2:
                    pe.wait_ge(g_min, h - 1)
                for c in range(2):
                    last = nc.tensor.matmul(ps[:, 2 * pair + c, 0:HALF], wg2[96:128, h * DK:(h + 1) * DK],
                                            zr[96:128, c * HALF:(c + 1) * HALF], start=True, stop=True)
                last.then_inc(g_mm, 1)
            with pe.Fori(0, M // 4) as i:
                for j in range(4):
                    pe.wait_ge(evac, gr.u0 + j - 1 + 4 * i)
                    slot_products(pe, gr.s0 + j, gpair(gr.u0 + j), xg_hi, xg_lo, i=i, per=4)
            pe.wait_ge(g_min, H)
            pe.wait_ge(evac, gkq.u0)

            def kq_unit(j):
                pe.wait_ge(evac, gkq.u0 + j)
                slot_products(pe, gkq.s0 + j, KQP, xg_hi, xg_lo)

            def core_products(h, t):
                j, p, y = h * TT + t, h % 2, t % 2
                cols = slice(t * P, (t + 1) * P)
                wait(pe, g_msk, 3 * (j - 1))
                nc.tensor.matmul(ps[:, sc_bank(y), 0:P], kinv[:, p, cols], q32[:, p, cols], start=True, stop=True)
                nc.tensor.matmul(ps[:, sc_bank(y), P:2 * P], k32[:, p, cols], q32[:, p, cols], start=True, stop=True)
                nc.tensor.matmul(ps[0:P // 2, sc_bank(y), 2 * P:2 * P + P // 2], k64[:, p, t, :], q64[:, p, t, :],
                                 start=True, stop=True).then_inc(g_sc, 1)
                wait(pe, g_S, j)
                nc.tensor.matmul(ps[:, KV_BANK, 0:DV], kend_tok[:, p, t, :], v_tok[:, t, h * DV:(h + 1) * DV],
                                 start=True, stop=True).then_inc(g_kv, 1)

            def core_output(h, t):
                j, y = h * TT + t, t % 2
                pe.wait_ge(g_msk, 3 * (j + 1))
                pe.wait_ge(g_S, j)
                wait(pe, g_oe, 2 * (j - 1))
                last = nc.tensor.matmul(ps[:, o_bank(y), 0:DV], msc[:, y, :], v_tok[:, t, h * DV:(h + 1) * DV],
                                        start=True, stop=(t == 0))
                if t:
                    last = nc.tensor.matmul(ps[:, o_bank(y), 0:DV], q128[:, h % 2, t * P:(t + 1) * P],
                                            S[:, t % 2, h, :], start=False, stop=True)
                last.then_inc(g_o, 1)

            def core(h, t0):
                pe.wait_ge(g_kq, KQ * (h + 1))
                pe.wait_ge(g_tre, 2 * M + 2 * h + 1)
                core_products(h, t0)
                core_products(h, t0 + 1)
                core_output(h, t0)
                core_output(h, t0 + 1)

            def sample_scores(h):
                pe.wait_ge(g_tre, 2 * M + 2 * h + 2)
                pe.wait_ge(g_kq, KQ * (h + 1))
                nc.tensor.matmul(ps[0:NS, T_BANK, 0:NS], kinv[:, h % 2, SEQ:T], q32[:, h % 2, SEQ:T],
                                 start=True, stop=True).then_inc(g_ssc, 1)

            for h in range(H + 1):
                if h < H:
                    kq_unit(2 * h)
                if h:
                    sample_scores(h - 1)
                    core(h - 1, 0)
                if h < H:
                    kq_unit(2 * h + 1)
                    pe.wait_ge(g_kq, KQ * h + 5)
                    wait(pe, g_smk, h)
                    for t in range(TT):
                        last = nc.tensor.transpose(ps[:, T_BANK, t * P:(t + 1) * P], acc[:, t * P:(t + 1) * P],
                                                   ident[:, :])
                    last.then_inc(g_tr, 1)
                if h:
                    core(h - 1, 2)
                if h < H:
                    pe.wait_ge(g_tre, 2 * M + 2 * h + 1)
                    nc.tensor.transpose(ps[0:NS, T_BANK, 0:P], k32[:, h % 2, SEQ:T], ident[:, :]).then_inc(g_tr, 1)

            pe.wait_ge(g_smk, H)
            pe.wait_ge(g_oe, 2 * TT * H)
            pe.wait_ge(g_msk, 3 * TT * H)
            pe.wait_ge(evac, gkq.u0 + 2 * H)
            for h in range(H):
                pe.wait_ge(g_st[h], 16)
                wait(pe, g_soe, 2 * (h - 1))
                nc.tensor.matmul(ps[0:NS, o_bank(h % 2), 0:DV], smsc[:, h, :], v_tok[:, TT, h * DV:(h + 1) * DV],
                                 start=True, stop=False)
                for s in range(NB):
                    last = nc.tensor.matmul(ps[0:NS, o_bank(h % 2), 0:DV], qsel[:, h, s * NS:(s + 1) * NS],
                                            st[:, h, s, :], start=False, stop=(s == NB - 1))
                last.then_inc(g_so, 1)
                if h == 0:
                    pe.wait_ge(g_kem, NB)
                for s in range(NB):
                    wait(pe, g_sS, NB * h + s - 3)
                    nc.tensor.matmul(ps[:, skv_bank(s), 0:DV], kem[:, s, h, :], v_tok[:, TT, h * DV:(h + 1) * DV],
                                     start=True, stop=True).then_inc(g_skv, 1)
            pe.wait_ge(g_soe, 2 * H)
            pe.wait_ge(g_sS, NB * H)
            for b in range(2 * H):
                pe.wait_ge(g_on, (TT + 1) * (b // VB + 1))
                wait(pe, g_y, b - 3)
                for t in range(TT):
                    nc.tensor.transpose(ps[:, 2 * (b % 4), t * P:(t + 1) * P], v_tok[:, t, b * P:(b + 1) * P],
                                        ident[:, :])
                nc.tensor.transpose(ps[:, 2 * (b % 4) + 1, 0:NS], v_tok[0:NS, TT, b * P:(b + 1) * P],
                                    ident[0:NS, 0:NS]).then_inc(g_ot, 1)
            pe.wait_ge(g_y, 2 * H)
            pe_square(pe, gwo, h_hi, h_lo, (h_split, gla_h0))

            pe_ffn(pe, f11)
            pe_stat(pe, 6, (f11.down.u0 + M + 3) % 4)
            pe.wait_ge(s_nv, 4 * 8 + 1)
            for m in range(M):
                pe.wait_ge(f_y, m + 1)
                for t in range(TT):
                    last = nc.tensor.transpose(ps[:, 2 * t + m // 4, (m % 4) * P:(m % 4 + 1) * P],
                                               x[:, m, t * P:(t + 1) * P], ident[:, :])
            last.then_inc(f_tr, 1)
            pe.wait_ge(f_e, 1)
            for m in range(M):
                last = nc.tensor.transpose(ps[0:NS, m // 4, (m % 4) * P:(m % 4 + 1) * P], x[:, m, SEQ:T], ident[:, :])
            last.then_inc(f_tr, 1)

        @block.scalar
        def _(act):
            act.dma_start(xin[:, 0:TT, :], x_prompt[0].rearrange("(t p) d -> p t d", p=P)).then_inc(s_in, 16)
            act.dma_start(xin[0:NS, TT, :], x_sample.rearrange("b t d -> (b t) d")).then_inc(s_in, 16)
            for row, v in PAR_ROWS:
                n = v.shape[0] // P
                act.dma_start(pin[row:row + n, :], v.rearrange("(m p) -> m p", p=P)).then_inc(s_in, 16)
            taps = conv_w_dw[0].rearrange("j (m p) -> (j m) p", p=P)
            for b in range(2):
                n = TAPS * M // 2
                act.dma_start(win[0:n, b, :], taps[b * n:(b + 1) * n, :]).then_inc(s_in, 16)
            act.wait_ge(s_par, 1)
            nc.scalar.activation(par[:, :], ps[:, 6, 0:NPAR], ACT.Copy).then_inc(s_parc, 1)
            nc.scalar.activation(wdw[:, :], ps[:, 7, 0:TAPS * M], ACT.Copy).then_inc(s_parc, 1)
            act.wait_ge(s_parc, 2)
            for n in range(AHEAD):
                high(act, n)
            for m in range(M):
                act_x_high(act, m, 0, m)
            act_ffn(act, f00)

            act_sqrt(act, 1)
            act.preload_act_table(ACT.Sigmoid)
            for m in range(4):
                act.wait_ge(c_tr, m + 1)
                dst = uext[:, 2 * m:2 * m + 2, HIST + SEQ:UEXT].rearrange("p m (b t) -> p m b t", t=SEG)
                for b in range(2):
                    last = nc.scalar.activation(
                        dst[:, b, :, 0:HIST],
                        ps[:, 4 + m % 2, b * NB * HIST:(b + 1) * NB * HIST].rearrange(
                            "p (b t) -> p b t", t=HIST), ACT.Copy)
                last.then_inc(c_tre, 1)
            for m in range(M):
                p = m % 2
                high(act, pw1.s0 + 2 * m + AHEAD)
                high(act, pw1.s0 + 2 * m + 1 + AHEAD)
                act.wait_ge(evac, pw1.u0 + 2 * m + 2)
                nc.scalar.activation(tb[:, p, :], tb[:, p, :], ACT.Sigmoid,
                                     bias=par[:, C_BPW1 + M + m:C_BPW1 + M + m + 1]).then_inc(a_done, 1)
                act.wait_ge(c_u, m + 1)
                nc.scalar.activation(tail[:, m, 0:HIST], uext[:, m, SEQ:SEQ + HIST], ACT.Copy)
                nc.scalar.activation(
                    tail[:, m, HIST:].rearrange("p (b t) -> p b t", t=DEC),
                    uext[:, m, HIST + SEQ:].rearrange("p (b t) -> p b t", t=SEG)[:, :, HIST:], ACT.Copy
                ).then_inc(c_tail, 1)
                nc.scalar.activation(cv[:, m, 0:SEQ], uext[:, m, 0:SEQ], ACT.Identity,
                                     bias=par[:, C_BDW + m:C_BDW + m + 1], scale=tap(0, m)).then_inc(c_tap0, 1)
                wait(act, c_pe, m - 1)
                for j in range(1, PE_TAPS + 1):
                    last = nc.scalar.activation(diag[:, m % 2, j - 1, :], ident[:, :], ACT.Copy, scale=tap(j, m))
                last.then_inc(c_diag, 1)
                wait(act, c_tap, (m - 1) * 2 * STEPS)
                for j in range(POOL_TAPS):
                    k = m * (POOL_TAPS - 1) + j - 1
                    if j:
                        wait(act, c_padd, k - PRODS + 1)
                    nc.scalar.activation(tap_prod[:, k % PRODS, :] if j else pool_sum[:, m % 2, :],
                                         uext[:, m, 1 + PE_TAPS + j:1 + PE_TAPS + j + SEQ], ACT.Copy,
                                         scale=tap(1 + PE_TAPS + j, m)).then_inc(c_prod, 1)
            act.preload_act_table(ACT.Sqrt)
            act.wait_ge(c_tt, 1)
            act.wait_ge(c_samp, 3 * M)
            for b in range(2):
                nc.scalar.activation(tail_out[0:HIST + NS, b * 512:(b + 1) * 512], ps[0:HIST + NS, 2 + b, :],
                                     ACT.Copy).then_inc(c_tte, 1)
            for m in range(M):
                act.wait_ge(c_mean, m + 1)
                wait(act, c_var, m - 3)
                nc.scalar.activation(squares(m), cv[:, m, :], ACT.Square).then_inc(c_sq, 1)
            act_sqrt(act, 2)
            act.preload_act_table(ACT.Silu)
            for m in range(M):
                act.wait_ge(c_norm, m + 1)
                nc.scalar.activation(ta[:, m % 2, :], ta[:, m % 2, :], ACT.Silu, bias=par[:, C_LNB + m:C_LNB + m + 1],
                                     scale=par[:, C_LNG + m:C_LNG + m + 1]).then_inc(a_done, 1)
                act.wait_ge(a_done, conv_a0 + M + m + 1)
                nc.scalar.activation(h_hi[:, m, :], ta[:, m % 2, :], ACT.Copy).then_inc(h_high, 1)
            with act.Fori(0, M // 4) as i:
                for j in range(4):
                    high(act, pw2.s0 + j + AHEAD, i, 4)
                    act_x_high(act, pw2.u0 + j + 4 * i, 2, j + 4 * i)

            act_ffn(act, f01)
            act_ffn(act, f10)

            act_sqrt(act, 5)
            high(act, gz.s0 + AHEAD)

            def to_tokens(k, dst):
                act.wait_ge(g_tr, k + 1)
                nc.scalar.activation(dst[:, 0:TT, :], ps[:, 2 * AUX0, :].rearrange("p (t n) -> p t n", t=TT),
                                     ACT.Copy).then_inc(g_tre, 1)
                nc.scalar.activation(dst[0:NS, TT, :], ps[0:NS, 2 * AUX0 + 1, 0:P], ACT.Copy).then_inc(g_tre, 1)

            act.wait_ge(g_const, 7)
            for j in range(M):
                high(act, gv.s0 + j + AHEAD)
                if j:
                    to_tokens(j - 1, v_tok[:, :, (j - 1) * P:j * P])
            to_tokens(M - 1, v_tok[:, :, (M - 1) * P:])
            act.preload_act_table_set("natural_log_exp_and_others")
            for h in range(H):
                act.wait_ge(g_mm, h + 1)
                nc.scalar.activation(halves(bc[:, h, :]), bank_pair((AUX1, AUX0)[h % 2]), ACT.Abs,
                                     bias=par[:, C_BG + h:C_BG + h + 1]).then_inc(g_abs, 1)
            act.wait_ge(g_abs, H)
            nc.scalar.activation(bc[:, :, :], bc[:, :, :], ACT.Exp, scale=-1.0).then_inc(g_abs, 1)
            act.wait_ge(g_abs, H + 1)
            nc.scalar.activation(bc[:, :, :], bc[:, :, :], ACT.Ln, bias=1.0).then_inc(g_abs, 1)
            act.preload_act_table(ACT.Silu)
            with act.Fori(0, M // 4) as i:
                for j in range(4):
                    high(act, gr.s0 + j + AHEAD, i, 4)
                    act.wait_ge(evac, gr.u0 + j + 1 + 4 * i)
                    nc.scalar.activation(rs[:, j + 4 * i, :], ta[:, j % 2, :], ACT.Silu).then_inc(a_done, 1)
            act.preload_act_table(ACT.Exp)
            act.wait_ge(g_fac, 7)
            act.wait_ge(g_min, 2 * H + 1)
            nc.scalar.activation(fac[:, :, :, :], fac[:, :, :, :], ACT.Exp, scale=1.0 / TAU)
            nc.scalar.activation(dec[:, :, :], bc[:, :, SEQ + DEC - 1:T:DEC], ACT.Exp, scale=1.0 / TAU).then_inc(g_dec, 1)

            def outputs(h, t0):
                for t in (t0, t0 + 1):
                    j = h * TT + t
                    act.wait_ge(g_o, j + 1)
                    nc.scalar.activation(v_tok[:, t, h * DV:(h + 1) * DV], ps[:, o_bank(t % 2), 0:DV],
                                         ACT.Copy).then_inc(g_oe, 1)
                    wait(act, g_oe, 2 * j)
                    nc.scalar.activation(ns[:, 0:DV], ps[:, o_bank(t % 2), 0:DV], ACT.Square,
                                         accum_out=ssq[:, t, h:h + 1]).then_inc(g_oe, 1)

            for h in range(H + 1):
                if h < H:
                    high(act, gkq.s0 + 2 * h + AHEAD)
                    wait(act, g_kq, KQ * (h - 1) + 7)
                    nc.scalar.activation(tb[:, 0, :], bc[:, h, :], ACT.Exp, scale=-1.0 / TAU).then_inc(g_exp, 1)
                    act.wait_ge(g_kq, KQ * h + 2)
                    nc.scalar.activation(tb[:, 1, :], tb[:, 1, :], ACT.Exp, scale=1.0 / TAU).then_inc(g_exp, 1)
                if h:
                    outputs(h - 1, 0)
                if h < H:
                    high(act, gkq.s0 + 2 * h + 1 + AHEAD)
                    act.wait_ge(g_kq, KQ * h + 3)
                    nc.scalar.activation(tb[:, 0, :], bc[:, h, :], ACT.Exp, scale=1.0 / TAU).then_inc(g_exp, 1)
                    act.wait_ge(g_tr, M + 2 * h + 1)
                    wait(act, g_kv, TT * (h - 1))
                    nc.scalar.activation(kend_tok[:, h % 2], ps[:, T_BANK, :].rearrange("p (t n) -> p t n", t=TT),
                                         ACT.Copy).then_inc(g_tre, 1)
                if h:
                    outputs(h - 1, 2)
                if h < H:
                    act.wait_ge(g_tr, M + 2 * h + 2)
                    nc.scalar.activation(kend_s[0:NS, h, :], ps[0:NS, T_BANK, 0:P], ACT.Copy).then_inc(g_tre, 1)
            act.preload_act_table(ACT.Sqrt)
            for h in range(H):
                act.wait_ge(g_so, h + 1)
                act.wait_ge(g_skv, NB * (h + 1))
                nc.scalar.activation(v_tok[0:NS, TT, h * DV:(h + 1) * DV], ps[0:NS, o_bank(h % 2), 0:DV],
                                     ACT.Copy).then_inc(g_soe, 1)
                act.wait_ge(g_oe, 2 * TT * H)
                wait(act, g_soe, 2 * h)
                nc.scalar.activation(ns[0:NS, 0:DV], ps[0:NS, o_bank(h % 2), 0:DV], ACT.Square,
                                     accum_out=ssq[0:NS, TT, h:h + 1]).then_inc(g_soe, 1)
            act.wait_ge(g_soe, 2 * H)
            act_sqrt(act, 6, (TT + 1) * H)
            act.wait_ge(s_rb, 7)

            def normed(h):
                for t in range(TT + 1):
                    rows = P if t < TT else NS
                    v = v_tok[0:rows, t, h * DV:(h + 1) * DV]
                    nc.scalar.activation(v, v, ACT.Copy, scale=rB[0:rows, t * H + h:t * H + h + 1]).then_inc(g_on, 1)

            normed(0)
            for h in range(H):
                if h < H - 1:
                    normed(h + 1)
                for b in range(VB * h, VB * (h + 1)):
                    act.wait_ge(g_y, b + 1)
                    nc.scalar.activation(h_hi[:, b, :], ta[:, b % 2, :], ACT.Copy).then_inc(h_high, 1)
            act.wait_ge(g_out, 16 * (H + 1))
            with act.Fori(0, M // 4) as i:
                for j in range(4):
                    high(act, gwo.s0 + j + AHEAD, i, 4)
                    act_x_high(act, gwo.u0 + j + 4 * i, 5, j + 4 * i)

            act_ffn(act, f11)
            act_sqrt(act, 8)
            act.wait_ge(f_tr, 1)
            for t in range(TT):
                nc.scalar.activation(yout[:, t, :].rearrange("p (c n) -> p c n", c=2), ps[:, 2 * t:2 * t + 2, :],
                                     ACT.Copy).then_inc(f_e, 1)
            act.wait_ge(f_tr, 2)
            nc.scalar.activation(yout[0:NS, TT, :].rearrange("p (c n) -> p c n", c=2), ps[0:NS, 0:2, :],
                                 ACT.Copy).then_inc(f_e, 1)

        @block.vector
        def _(dve):
            for m in range(M):
                dve.wait_ge(u_init, m + 1)
                nc.vector.tensor_copy(x[:, m, 0:SEQ], ps[:, 2 * (m % 4), 0:SEQ])
                nc.vector.tensor_copy(x[:, m, SEQ:T], ps[:, 2 * (m % 4) + 1, 0:NS]).then_inc(evac, 1)
                if m % 2:
                    low(dve, m // 2)
            dve.wait_ge(s_parc, 2)
            for m in range(M):
                dve_x_split(dve, 0, m)
            dve_ffn(dve, f00)

            dve_rsqrt(dve, 1, 3, (s_stat, 2))
            dve.wait_ge(c_zero, 1)
            dve.wait_ge(c_tre, 4)

            def conv_block(m):
                j = DVE_TAP0
                dve.wait_ge(c_tap0, m + 1)
                for step in range(STEPS):
                    for half in range(2):
                        n = SEQ // 2
                        part = cv[:, m, half * n:(half + 1) * n]
                        if step:
                            dve.wait_ge(c_tap, 2 * (m * STEPS + step) - 1 + half)
                        if step == PSUM_STEP:
                            dve.wait_ge(c_pe, m + 1)
                            last = nc.vector.tensor_tensor(part, part, ps[:, 4 + m % 2, half * n:(half + 1) * n],
                                                           ALU.add)
                        elif step == STEPS - 1:
                            dve.wait_ge(c_padd, (m + 1) * (POOL_TAPS - 1))
                            last = nc.vector.tensor_tensor(part, part, pool_sum[:, m % 2, half * n:(half + 1) * n],
                                                           ALU.add)
                        else:
                            last = nc.vector.scalar_tensor_tensor(
                                out=part, in0=uext[:, m, j + half * n:j + (half + 1) * n], scalar=tap(j, m),
                                in1=part, op0=ALU.mult, op1=ALU.add)
                        last.then_inc(c_tap, 1)
                    if step != PSUM_STEP:
                        j += 1

            for m in range(M):
                p = m % 2
                n = pw1.s0 + 2 * m
                dve.wait_ge(w_done, n + 1)
                nc.vector.tensor_tensor(halves(ta[:, p, :]), bank_pair(0), halves(rB[:, :]), ALU.mult).then_inc(evac, 1)
                low(dve, n + AHEAD)
                dve.wait_ge(w_done, n + 2)
                nc.vector.tensor_tensor(halves(tb[:, p, :]), bank_pair(1), halves(rB[:, :]), ALU.mult).then_inc(evac, 1)
                low(dve, n + 1 + AHEAD)
                dve.wait_ge(a_done, conv_a0 + m + 1)
                bias = par[:, C_BPW1 + m:C_BPW1 + m + 1]
                samples = uext[:, m, HIST + SEQ:].rearrange("p (b t) -> p b t", t=SEG)
                nc.vector.scalar_tensor_tensor(out=uext[:, m, HIST:HIST + SEQ], in0=ta[:, p, 0:SEQ], scalar=bias,
                                               in1=tb[:, p, 0:SEQ], op0=ALU.add, op1=ALU.mult)
                nc.vector.scalar_tensor_tensor(
                    out=samples[:, :, HIST:], in0=ta[:, p, SEQ:T].rearrange("p (b t) -> p b t", t=DEC), scalar=bias,
                    in1=tb[:, p, SEQ:T].rearrange("p (b t) -> p b t", t=DEC), op0=ALU.add,
                    op1=ALU.mult).then_inc(c_u, 1)
                dve.wait_ge(c_u, m + 1)
                taps_of_block = wdw[:, :].rearrange("p (j m) -> p j m", m=M)[:, :, m]
                for t in range(DEC):
                    last = nc.vector.tensor_tensor(
                        prod[:, :, :].rearrange("p (b t) j -> p b t j", t=DEC)[:, :, t, :],
                        samples[:, :, t:t + TAPS],
                        taps_of_block.rearrange("p (o j) -> p o j", o=1).to_broadcast([P, NB, TAPS]), ALU.mult)
                last.then_inc(c_samp, 1)
                dve.wait_ge(c_samp, 3 * m + 1)
                nc.vector.tensor_reduce(cv[:, m, SEQ:T], prod[:, :, :], AX_X, ALU.add).then_inc(c_samp, 1)
                dve.wait_ge(c_samp, 3 * m + 2)
                nc.vector.tensor_scalar(cv[:, m, SEQ:T], cv[:, m, SEQ:T], par[:, C_BDW + m:C_BDW + m + 1], None,
                                        ALU.add).then_inc(c_samp, 1)
                if m:
                    conv_block(m - 1)
            conv_block(M - 1)
            dve.wait_ge(c_mu, M)
            for m in range(M):
                nc.vector.tensor_tensor(halves(cv[:, m, :]), halves(cv[:, m, :]), bank_pair(3),
                                        ALU.subtract).then_inc(c_mean, 1)
            dve_rsqrt(dve, 2, 0, (c_var, M))
            for m in range(M + 1):
                if m < M:
                    if m >= 2:
                        dve.wait_ge(h_split, conv_h0 + m - 1)
                    nc.vector.tensor_tensor(ta[:, m % 2, :], cv[:, m, :], rB[:, :], ALU.mult).then_inc(c_norm, 1)
                if m:
                    dve.wait_ge(h_high, conv_h0 + m)
                    nc.vector.tensor_tensor(h_lo[:, m - 1, :], ta[:, (m - 1) % 2, :],
                                            h_hi[:, m - 1, :].bitcast(F32), ALU.subtract).then_inc(h_split, 1)
            with dve.Fori(0, M // 4) as i:
                for j in range(4):
                    m = j + 4 * i
                    low(dve, pw2.s0 + j + AHEAD, i, 4)
                    dve.wait_ge(w_done, pw2.s0 + j + 1 + 4 * i)
                    nc.vector.scalar_tensor_tensor(
                        out=halves(x[:, m, :]), in0=bank_pair((pw2.u0 + j) % 4),
                        scalar=par[:, bass.ds(C_BPW2 + m, 1)], in1=halves(x[:, m, :]), op0=ALU.add,
                        op1=ALU.add).then_inc(evac, 1)
                    dve_x_split(dve, 2, m)

            dve_ffn(dve, f01)
            dve_ffn(dve, f10)

            dve_rsqrt(dve, 5, AUX1, (s_stat, 5))
            dve.wait_ge(w_done, gz.s0 + 1)
            nc.vector.tensor_tensor(halves(zr[:, :]), bank_pair(gpair(gz.u0)), halves(rB[:, :]),
                                    ALU.mult).then_inc(evac, 1)
            low(dve, gz.s0 + AHEAD)
            for j in range(M):
                dve.wait_ge(w_done, gv.s0 + j + 1)
                wait(dve, g_tr, j - 1)
                nc.vector.tensor_tensor(halves(ta[:, j % 2, :]), bank_pair(gpair(gv.u0 + j)), halves(rB[:, :]),
                                        ALU.mult).then_inc(evac, 1)
                low(dve, gv.s0 + j + AHEAD)
            for h in range(H):
                dve.wait_ge(g_abs, h + 1)
                nc.vector.tensor_scalar(halves(la[:, h, :]), bank_pair((AUX1, AUX0)[h % 2]),
                                        par[:, C_BG + h:C_BG + h + 1], 0.0, ALU.add, ALU.min).then_inc(g_min, 1)
            dve.wait_ge(g_abs, H + 2)
            dve.wait_ge(g_min, H)
            nc.vector.tensor_tensor(la[:, :, :], la[:, :, :], bc[:, :, :], ALU.subtract).then_inc(g_min, 1)
            dve.wait_ge(g_min, H + 1)
            dve.wait_ge(g_const, 15)
            for h in range(H):
                nc.vector.tensor_tensor_scan(bc[:, h, :], reset[:, :], la[:, h, :], 0.0, ALU.mult,
                                             ALU.add).then_inc(g_min, 1)
            dve.wait_ge(g_min, 2 * H + 1)

            def chunk_total(g):
                return bc[:, :, 0:SEQ].rearrange("p h (t g c) -> p h t g c", g=G, c=CH)[:, :, :, g, CH - 1]

            nc.vector.tensor_copy(fac[:, :, :, F_E + 1], chunk_total(0)).then_inc(g_fac, 1)
            nc.vector.tensor_copy(fac[:, :, :, F_X], chunk_total(1)).then_inc(g_fac, 1)
            nc.vector.tensor_copy(fac[:, :, :, F_X + G - 1], chunk_total(2)).then_inc(g_fac, 1)
            for g in range(1, G):
                dve.wait_ge(g_fac, g + 2)
                nc.vector.tensor_tensor(fac[:, :, :, F_E + g + 1], fac[:, :, :, F_E + g], chunk_total(g),
                                        ALU.add).then_inc(g_fac, 1)
            dve.wait_ge(g_fac, 6)
            nc.vector.tensor_tensor(fac[:, :, :, F_R:F_R + G],
                                    fac[:, :, :, F_E + G:F_E + G + 1].to_broadcast([P, H, TT, G]),
                                    fac[:, :, :, F_E + 1:F_E + 1 + G], ALU.subtract).then_inc(g_fac, 1)
            with dve.Fori(0, M // 4) as i:
                for j in range(4):
                    dve.wait_ge(w_done, gr.s0 + j + 1 + 4 * i)
                    dve.wait_ge(a_done, gla_a0 + j - 1 + 4 * i)
                    dve.wait_ge(g_tr, M)
                    nc.vector.tensor_tensor(halves(ta[:, j % 2, :]), bank_pair(gpair(gr.u0 + j)), halves(rB[:, :]),
                                            ALU.mult).then_inc(evac, 1)
                    low(dve, gr.s0 + j + AHEAD, i, 4)
            dve.wait_ge(a_done, gla_a0 + M)

            def key_steps(h):
                p, n0 = h % 2, KQ * h
                wait(dve, g_o, TT * (h - 1))
                dve.wait_ge(g_exp, 3 * h + 1)
                dve.wait_ge(evac, gkq.u0 + 2 * h + 1)
                nc.vector.tensor_tensor(kinv[:, p, :], ta[:, 0, :], tb[:, 0, :], ALU.mult).then_inc(g_kq, 1)
                dve.wait_ge(g_exp, 3 * h + 2)
                nc.vector.tensor_tensor(k32[:, p, :], ta[:, 0, :], tb[:, 1, :], ALU.mult).then_inc(g_kq, 1)
                dve.wait_ge(g_kq, n0 + 4)
                dve.wait_ge(g_dec, 1)
                wait(dve, g_tr, M + 2 * h - 1 if h else 0)
                nc.vector.tensor_tensor(by_chunk(acc[:, 0:SEQ]), by_chunk(k32[:, p, 0:SEQ]), factor(h, F_R),
                                        ALU.mult).then_inc(g_kq, 1)
                nc.vector.tensor_tensor(k64[:, p].rearrange("p t (g c) -> p t g c", c=CH),
                                        by_chunk(k32[:, p, 0:SEQ])[:, :, 0:G // 2, :], factor(h, F_X, 0, G // 2),
                                        ALU.mult).then_inc(g_kq, 1)

            def query_steps(h):
                p, n0 = h % 2, KQ * h
                dve.wait_ge(g_exp, 3 * h + 3)
                dve.wait_ge(evac, gkq.u0 + 2 * h + 2)
                nc.vector.scalar_tensor_tensor(out=q32[:, p, :], in0=ta[:, 1, :], scalar=float(DK) ** -0.5,
                                               in1=tb[:, 0, :], op0=ALU.mult, op1=ALU.mult).then_inc(g_kq, 1)
                dve.wait_ge(g_kq, n0 + 7)
                nc.vector.tensor_tensor(by_chunk(q128[:, p, P:SEQ]), by_chunk(q32[:, p, P:SEQ]), factor(h, F_E, 1),
                                        ALU.mult).then_inc(g_kq, 1)
                nc.vector.tensor_tensor(q64[:, p].rearrange("p t (g c) -> p t g c", c=CH),
                                        by_chunk(q32[:, p, 0:SEQ])[:, :, G // 2:G, :],
                                        factor(h, F_X + G // 2, 0, G // 2), ALU.mult).then_inc(g_kq, 1)
                nc.vector.tensor_copy(qsel[:, h, :].rearrange("p (s c) -> p s c", c=SEL)[:, :, 0:DEC],
                                      q32[:, p, SEQ:T].rearrange("p (s c) -> p s c", c=DEC)).then_inc(g_kq, 1)

            def core_steps(h, t0):
                for t in (t0, t0 + 1):
                    j, y = h * TT + t, t % 2
                    dve.wait_ge(g_sc, j + 1)
                    wait(dve, g_o, j - 1)
                    nc.vector.copy_predicated(msc[:, y, :], mask[:, 0, :].bitcast(I32),
                                              ps[:, sc_bank(y), 0:P]).then_inc(g_msk, 1)
                    dve.wait_ge(g_msk, 3 * j + 1)
                    nc.vector.copy_predicated(msc[:, y, :], mask[:, 1, :].bitcast(I32),
                                              ps[:, sc_bank(y), P:2 * P]).then_inc(g_msk, 1)
                    dve.wait_ge(g_msk, 3 * j + 2)
                    nc.vector.tensor_copy(msc[0:P // 2, y, P // 2:P],
                                          ps[0:P // 2, sc_bank(y), 2 * P:2 * P + P // 2]).then_inc(g_msk, 1)
                    dve.wait_ge(g_kv, j + 1)
                    if t >= 2:
                        dve.wait_ge(g_o, j)
                    if t == 0:
                        nc.vector.tensor_copy(S[:, 1, h, :], ps[:, KV_BANK, 0:DV]).then_inc(g_S, 1)
                    else:
                        dve.wait_ge(g_S, j)
                        nc.vector.scalar_tensor_tensor(
                            out=S[:, (t + 1) % 2, h, :], in0=S[:, t % 2, h, :],
                            scalar=fac[:, h, t, F_E + G:F_E + G + 1], in1=ps[:, KV_BANK, 0:DV], op0=ALU.mult,
                            op1=ALU.add).then_inc(g_S, 1)

            dve.wait_ge(g_const, 24)
            for h in range(H + 1):
                if h < H:
                    wait(dve, g_kq, KQ * h)
                    for a, n, c in ((0, SEQ // CH, CH), (SEQ, NB, DEC)):
                        b = bc[:, h, a:a + n * c].rearrange("p (n c) -> p n c", c=c)
                        last = nc.vector.tensor_tensor(tb[:, 1, a:a + n * c].rearrange("p (n c) -> p n c", c=c),
                                                       b[:, :, c - 1:c].to_broadcast([P, n, c]), b, ALU.subtract)
                        last.then_inc(g_kq, 1)
                    dve.wait_ge(w_done, gkq.s0 + 2 * h + 1)
                    nc.vector.tensor_tensor(halves(ta[:, 0, :]), bank_pair(KQP), halves(rB[:, :]),
                                            ALU.mult).then_inc(evac, 1)
                    low(dve, gkq.s0 + 2 * h + AHEAD)
                if h:
                    dve.wait_ge(g_ssc, h)
                    nc.vector.copy_predicated(smsc[0:NS, h - 1, :], smask[0:NS, :].bitcast(I32),
                                              ps[0:NS, T_BANK, 0:NS]).then_inc(g_smk, 1)
                    core_steps(h - 1, 0)
                if h < H:
                    key_steps(h)
                    dve.wait_ge(w_done, gkq.s0 + 2 * h + 2)
                    nc.vector.tensor_tensor(halves(ta[:, 1, :]), bank_pair(KQP), halves(rB[:, :]),
                                            ALU.mult).then_inc(evac, 1)
                    low(dve, gkq.s0 + 2 * h + 1 + AHEAD)
                if h:
                    core_steps(h - 1, 2)
                if h < H:
                    query_steps(h)
            dve.wait_ge(g_tre, 2 * M + 2 * H)
            dve.wait_ge(g_o, TT * H)
            for s in range(NB):
                nc.vector.tensor_scalar(kem[:, s], kend_s[:, :, :], bmask[:, s:s + 1], None, ALU.mult).then_inc(g_kem, 1)
            for h in range(H):
                for s in range(NB):
                    dve.wait_ge(g_skv, NB * h + s + 1)
                    nc.vector.scalar_tensor_tensor(
                        out=st[:, h, s, :], in0=st[:, h, s, :], scalar=dec[:, h, s:s + 1],
                        in1=ps[:, skv_bank(s), 0:DV], op0=ALU.mult, op1=ALU.add).then_inc(g_sS, 1)
            dve.wait_ge(g_oe, 2 * TT * H)
            dve_rsqrt(dve, 6, None, (g_soe, 2 * H), (TT + 1) * H)
            for b in range(2 * H + 1):
                if b < 2 * H:
                    wait(dve, h_split, gla_h0 + b - 1 if b >= 2 else 0)
                    dve.wait_ge(g_ot, b + 1)
                    for bank, c0, c1 in ((2 * (b % 4), 0, SEQ), (2 * (b % 4) + 1, SEQ, T)):
                        last = nc.vector.scalar_tensor_tensor(
                            out=ta[:, b % 2, c0:c1], in0=ps[:, bank, 0:c1 - c0],
                            scalar=par[:, C_ON + b % VB:C_ON + b % VB + 1], in1=rs[:, b, c0:c1], op0=ALU.mult,
                            op1=ALU.mult)
                    last.then_inc(g_y, 1)
                if b:
                    dve.wait_ge(h_high, gla_h0 + b)
                    nc.vector.tensor_tensor(h_lo[:, b - 1, :], ta[:, (b - 1) % 2, :], h_hi[:, b - 1, :].bitcast(F32),
                                            ALU.subtract).then_inc(h_split, 1)
            with dve.Fori(0, M // 4) as i:
                for j in range(4):
                    m = j + 4 * i
                    low(dve, gwo.s0 + j + AHEAD, i, 4)
                    dve.wait_ge(w_done, gwo.s0 + j + 1 + 4 * i)
                    nc.vector.tensor_tensor(halves(x[:, m, :]), bank_pair((gwo.u0 + j) % 4), halves(x[:, m, :]),
                                            ALU.add).then_inc(evac, 1)
                    dve_x_split(dve, 5, m)

            dve_ffn(dve, f11)
            dve_rsqrt(dve, 8, (f11.down.u0 + M + 3) % 4, (s_stat, 7))
            for m in range(M):
                nc.vector.scalar_tensor_tensor(out=x[:, m, :], in0=x[:, m, :], scalar=par[:, 6 * M + m:6 * M + m + 1],
                                               in1=rB[:, :], op0=ALU.mult, op1=ALU.mult).then_inc(f_y, 1)


OUTS = [("y_prompt", (1, 512, 1024)), ("y_sample", (8, 4, 1024)), ("new_conv_prompt", (1, 1, 30, 1024)),
        ("new_gla_prompt", (1, 1, 4, 128, 256)), ("new_conv_sample", (1, 8, 30, 1024)),
        ("new_gla_sample", (1, 8, 4, 128, 256))]


def kernel(**inputs):
    import concourse.bacc as bacc
    import numpy as np
    from concourse.bass_utils import run_bass_kernel_spmd

    nc = bacc.Bacc("TRN2", target_bir_lowering=False, num_devices=1)
    arrays, args = {}, {}
    for name, value in inputs.items():
        a = np.ascontiguousarray(value)
        arrays[f"in_{name}"] = a
        args[name] = nc.dram_tensor(f"in_{name}", a.shape, mybir.dt.from_np(a.dtype), kind="ExternalInput").ap()
    for name, shape in OUTS:
        args[name] = nc.dram_tensor(f"out_{name}", shape, F32, kind="ExternalOutput").ap()
    build(nc, **args)
    r = run_bass_kernel_spmd(nc, [arrays], core_ids=[0])
    return tuple(r.results[0][f"out_{name}"] for name, _ in OUTS)
```
